# Optimizing a Trainium2 kernel written in Bass

```python
import math
import jax, jax.numpy as jnp
from jax import lax
import numpy as np

D_MODEL = 2048
BATCH = 1
SEQ = 512
DEPTH = 1

D_MIX = D_MODEL
D_ATTN = D_MIX // 2
D_CONV = D_MIX - D_ATTN
ATTN_HEAD_DIM = 64
ATTN_VALUE_DIM = 2 * ATTN_HEAD_DIM
N_ATTN_HEADS = D_ATTN // ATTN_VALUE_DIM
QK_COLS = N_ATTN_HEADS * 2 * ATTN_HEAD_DIM
V_COLS = N_ATTN_HEADS * ATTN_VALUE_DIM
GLU_COLS = 2 * D_CONV
D_IN_PROJ = 2 * QK_COLS + V_COLS + GLU_COLS
CONV_WIDTH = 31
QUERY_BLOCK = 128
REL_BUCKETS = 32
REL_MAX_EXACT = REL_BUCKETS // 2
REL_MAX_DISTANCE = 128
PEER_HEADS = 8
PEER_N_KEYS = 128
PEER_N_EXPERTS = PEER_N_KEYS * PEER_N_KEYS
PEER_KEY_DIM = 256
PEER_HALF_DIM = PEER_KEY_DIM // 2
PEER_TOPK = 16
PEER_TOKEN_BLOCK = 128
LN_EPS = 1e-5
DEEPNORM_ALPHA = (2.0 * DEPTH) ** 0.25
DEEPNORM_BETA = (8.0 * DEPTH) ** -0.25

kernel_name = "hybrid_diffattn_conformer_peer_deepnorm"

def _layer_norm(x, g, b):
    xf = x.astype(jnp.float32)
    mu = jnp.mean(xf, axis=-1, keepdims=True)
    var = jnp.mean(jnp.square(xf - mu), axis=-1, keepdims=True)
    y = (xf - mu) * lax.rsqrt(var + LN_EPS)
    return (y * g.astype(jnp.float32) + b.astype(jnp.float32)).astype(x.dtype)

def _rms_norm(x, g):
    xf = x.astype(jnp.float32)
    y = xf * lax.rsqrt(jnp.mean(jnp.square(xf), axis=-1, keepdims=True) + LN_EPS)
    return (y * g.astype(jnp.float32)).astype(x.dtype)

def _t5_bucket(dist):
    n_f = jnp.maximum(dist, 1).astype(jnp.float32)
    large = REL_MAX_EXACT + (
        jnp.log(n_f / REL_MAX_EXACT) / math.log(REL_MAX_DISTANCE / REL_MAX_EXACT)
        * (REL_BUCKETS - REL_MAX_EXACT)).astype(jnp.int32)
    large = jnp.minimum(large, REL_BUCKETS - 1)
    return jnp.where(dist < REL_MAX_EXACT, dist, large)

def _diff_attention(q, k, v, lam, rel_bias):
    B, S = q.shape[0], q.shape[1]
    nb = S // QUERY_BLOCK
    q_blocks = q.reshape(B, nb, QUERY_BLOCK, N_ATTN_HEADS, 2, ATTN_HEAD_DIM).transpose(1, 0, 3, 4, 2, 5)
    kt = k.transpose(0, 2, 3, 1, 4)
    vt = v.transpose(0, 2, 1, 3)
    key_pos = jnp.arange(S, dtype=jnp.int32)
    scale = ATTN_HEAD_DIM ** -0.5

    def block(args):
        q_blk, start = args
        q_pos = start + jnp.arange(QUERY_BLOCK, dtype=jnp.int32)
        dist = q_pos[:, None] - key_pos[None, :]
        bias = rel_bias[_t5_bucket(jnp.maximum(dist, 0))].transpose(2, 0, 1)
        logits = jnp.einsum('bhcqd,bhckd->bhcqk', q_blk, kt).astype(jnp.float32) * scale
        logits = logits + bias[None, :, None].astype(jnp.float32)
        logits = jnp.where((dist >= 0)[None, None, None], logits, -jnp.inf)
        p = jax.nn.softmax(logits, axis=-1)
        p = (p[:, :, 0] - lam * p[:, :, 1]).astype(vt.dtype)
        return jnp.einsum('bhqk,bhkd->bqhd', p, vt)

    starts = jnp.arange(nb, dtype=jnp.int32) * QUERY_BLOCK
    out = lax.map(block, (q_blocks, starts))
    return out.transpose(1, 0, 2, 3, 4).reshape(B, S, N_ATTN_HEADS, ATTN_VALUE_DIM)

def _conformer_conv(glu_in, b_glu, conv_w, conv_b, ln_g, ln_b):
    h = glu_in + b_glu
    a, gate = jnp.split(h, 2, axis=-1)
    h = a * jax.nn.sigmoid(gate)
    h = lax.conv_general_dilated(
        h, conv_w.reshape(CONV_WIDTH, 1, D_CONV).astype(h.dtype),
        window_strides=(1,), padding=[(CONV_WIDTH - 1, 0)],
        dimension_numbers=('NWC', 'WIO', 'NWC'), feature_group_count=D_CONV) + conv_b
    return jax.nn.silu(_layer_norm(h, ln_g, ln_b))

def _peer(x, wq, sub_keys, u_table, v_table):
    B, S, D = x.shape
    tokens = x.reshape(-1, PEER_TOKEN_BLOCK, D)

    def chunk(xc):
        T = xc.shape[0]
        q = (xc @ wq).reshape(T, PEER_HEADS, 2, PEER_HALF_DIM)
        s = jnp.einsum('thcd,hcnd->thcn', q, sub_keys)
        s1, i1 = lax.top_k(s[:, :, 0], PEER_TOPK)
        s2, i2 = lax.top_k(s[:, :, 1], PEER_TOPK)
        cand = (s1[..., :, None] + s2[..., None, :]).reshape(T, PEER_HEADS, PEER_TOPK * PEER_TOPK)
        sc, ci = lax.top_k(cand, PEER_TOPK)
        e = (jnp.take_along_axis(i1, ci // PEER_TOPK, axis=-1) * PEER_N_KEYS
             + jnp.take_along_axis(i2, ci % PEER_TOPK, axis=-1))
        g = jax.nn.softmax(sc.astype(jnp.float32), axis=-1).astype(xc.dtype)
        u = u_table[e]
        act = jax.nn.gelu(jnp.einsum('td,thkd->thk', xc, u), approximate=False)
        return jnp.einsum('thk,thkd->td', g * act, v_table[e])

    return lax.map(chunk, tokens).reshape(B, S, D)

def setup_inputs(seed: int = 0) -> dict:
    key = jax.random.key(seed)
    ks = jax.random.split(key, 24)
    f32 = jnp.float32
    nrm = lambda k, shape: jax.random.normal(k, shape, f32)
    L = DEPTH
    return {
        "x": nrm(ks[0], (BATCH, SEQ, D_MODEL)),
        "w_in": nrm(ks[1], (L, D_MODEL, D_IN_PROJ)) * D_MODEL ** -0.5,
        "b_glu": 0.02 * nrm(ks[2], (L, GLU_COLS)),
        "conv_w": nrm(ks[3], (L, CONV_WIDTH, D_CONV)) * CONV_WIDTH ** -0.5,
        "conv_b": 0.02 * nrm(ks[4], (L, D_CONV)),
        "conv_ln_g": 1.0 + 0.02 * nrm(ks[5], (L, D_CONV)),
        "conv_ln_b": 0.02 * nrm(ks[6], (L, D_CONV)),
        "lambda_q1": 0.1 * nrm(ks[7], (L, ATTN_HEAD_DIM)),
        "lambda_k1": 0.1 * nrm(ks[8], (L, ATTN_HEAD_DIM)),
        "lambda_q2": 0.1 * nrm(ks[9], (L, ATTN_HEAD_DIM)),
        "lambda_k2": 0.1 * nrm(ks[10], (L, ATTN_HEAD_DIM)),
        "subln_g": 1.0 + 0.02 * nrm(ks[11], (L, ATTN_VALUE_DIM)),
        "rel_bias": 0.1 * nrm(ks[12], (REL_BUCKETS, N_ATTN_HEADS)),
        "w_out": nrm(ks[13], (L, D_MIX, D_MODEL)) * (D_MIX ** -0.5) * DEEPNORM_BETA,
        "ln1_g": 1.0 + 0.02 * nrm(ks[14], (L, D_MODEL)),
        "ln1_b": 0.02 * nrm(ks[15], (L, D_MODEL)),
        "peer_wq": nrm(ks[16], (L, D_MODEL, PEER_HEADS * PEER_KEY_DIM)) * D_MODEL ** -0.5,
        "peer_keys": nrm(ks[17], (L, PEER_HEADS, 2, PEER_N_KEYS, PEER_HALF_DIM)) * PEER_HALF_DIM ** -0.5,
        "peer_u": nrm(ks[18], (L, PEER_N_EXPERTS, D_MODEL)) * D_MODEL ** -0.5,
        "peer_v": nrm(ks[19], (L, PEER_N_EXPERTS, D_MODEL)) * DEEPNORM_BETA,
        "ln2_g": 1.0 + 0.02 * nrm(ks[20], (L, D_MODEL)),
        "ln2_b": 0.02 * nrm(ks[21], (L, D_MODEL)),
    }

def reference(x, w_in, b_glu, conv_w, conv_b, conv_ln_g, conv_ln_b,
              lambda_q1, lambda_k1, lambda_q2, lambda_k2, subln_g, rel_bias,
              w_out, ln1_g, ln1_b, peer_wq, peer_keys, peer_u, peer_v,
              ln2_g, ln2_b):
    B, S, _ = x.shape
    for layer in range(DEPTH):
        proj = jnp.einsum('bsd,de->bse', x, w_in[layer])
        q = proj[..., :QK_COLS].reshape(B, S, N_ATTN_HEADS, 2, ATTN_HEAD_DIM)
        k = proj[..., QK_COLS:2 * QK_COLS].reshape(B, S, N_ATTN_HEADS, 2, ATTN_HEAD_DIM)
        v = proj[..., 2 * QK_COLS:2 * QK_COLS + V_COLS].reshape(B, S, N_ATTN_HEADS, ATTN_VALUE_DIM)
        glu_in = proj[..., 2 * QK_COLS + V_COLS:]

        lambda_init = 0.8 - 0.6 * math.exp(-0.3 * layer)
        lam = (jnp.exp(jnp.sum(lambda_q1[layer].astype(jnp.float32) * lambda_k1[layer].astype(jnp.float32)))
               - jnp.exp(jnp.sum(lambda_q2[layer].astype(jnp.float32) * lambda_k2[layer].astype(jnp.float32)))
               + lambda_init)
        attn = _diff_attention(q, k, v, lam, rel_bias)
        attn = (_rms_norm(attn, subln_g[layer]) * (1.0 - lambda_init)).reshape(B, S, D_ATTN)

        conv = _conformer_conv(glu_in, b_glu[layer], conv_w[layer], conv_b[layer],
                               conv_ln_g[layer], conv_ln_b[layer])

        mix = jnp.einsum('bse,ed->bsd', jnp.concatenate([attn, conv], axis=-1), w_out[layer])
        x = _layer_norm(DEEPNORM_ALPHA * x + mix, ln1_g[layer], ln1_b[layer])

        ffn = _peer(x, peer_wq[layer], peer_keys[layer], peer_u[layer], peer_v[layer])
        x = _layer_norm(DEEPNORM_ALPHA * x + ffn, ln2_g[layer], ln2_b[layer])
    return x


_drawn_inputs = setup_inputs


def setup_inputs(seed=0):
    import zlib

    import numpy as np

    out = dict(_drawn_inputs(seed))
    spreads = {}
    factors = {'b_glu': 2.91,
     'conv_ln_g': 2.832,
     'conv_ln_b': 3.117,
     'lambda_q2': 3.453,
     'lambda_k2': 5.172,
     'ln2_g': 8.247,
     'ln2_b': 7.945,
     'lambda_q1': 3.561,
     'lambda_k1': 4.627,
     'subln_g': 2.932}
    for name, (base, spread) in spreads.items():
        noise = np.random.default_rng([zlib.crc32(name.encode()), seed]).standard_normal(out[name].shape)
        drawn = base * np.exp(spread * noise) if base else spread * noise
        out[name] = __import__('jax').numpy.asarray(drawn.astype(out[name].dtype))
    for name, factor in factors.items():
        out[name] = (out[name] * factor).astype(out[name].dtype)
    return out
```

```python
import math
from contextlib import ExitStack, contextmanager

import numpy as np

import concourse.bass as bass
from concourse import mybir
from concourse.alu_op_type import AluOpType as ALU

F32 = mybir.dt.float32
F32R = mybir.dt.float32r
BF16 = mybir.dt.bfloat16
U32 = mybir.dt.uint32
ACT = mybir.ActivationFunctionType
AX_X = mybir.AxisListType.X

P = 128
T = 512
TT = T // P
D = 2048
KT = D // P
CB = 512
HEADS = 8
DH = 64
DC = 1024
CT = DC // P
TAPS = 31
LN_DVE = 1408
BUCKETS = 32
MAX_EXACT = BUCKETS // 2
MAX_DISTANCE = 128
PH = 8
NK = 128
TOPK = 16
HC = 2 * PH
EPS = 1e-5
ALPHA = 2.0 ** 0.25
LAMBDA_INIT = 0.8 - 0.6 * math.exp(-0.3 * 0)
MASKED = -1.0e30
TAKEN = -3.0e38

QK_COLS = HEADS * 2 * DH
V_COL0 = 2 * QK_COLS
GLU_COL0 = V_COL0 + HEADS * 2 * DH

PIECES = 4
LOADS = KT // PIECES
B_QK, B_V, B_OUT, B_WQ, BLOCKS = 4, 8, 10, 14, 18
HK = KT // 2
HALF_LOADS = LOADS // 2
FILL = (1, 1, 1, 1, 1, 1, 1, 0)
GROUPS = NK // PIECES

ROUTE_CHUNKS = 6
GATE_CHUNKS = 8
QUADS = P // 4 // GATE_CHUNKS
STORE_CHUNKS = 8
AHEAD = TT * (ROUTE_CHUNKS + GATE_CHUNKS) + STORE_CHUNKS
AHEAD_GROUPS = AHEAD // PIECES

BV = 640
SPAN = T + P - 1


def bucket_ranges():
    out = [[] for _ in range(BUCKETS)]
    for n in range(T):
        b = n
        if n >= MAX_EXACT:
            b = MAX_EXACT + int(math.log(n / MAX_EXACT) / math.log(MAX_DISTANCE / MAX_EXACT) * (BUCKETS - MAX_EXACT))
            b = min(b, BUCKETS - 1)
        out[b].append(n)
    return [(o[0], o[-1]) if o else None for o in out]


class Steps:

    def __init__(self, eng, sem, start=0):
        self.eng, self.sem, self.total = eng, sem, start

    def __call__(self, ins):
        self.total = self.total + 1
        return ins.then_inc(self.sem, 1)

    def wait(self, behind=0):
        self.eng.wait_ge(self.sem, self.total - behind)

    @contextmanager
    def loop(self, start, end, per):
        before = self.total
        with self.eng.Fori(start, end) as i:
            self.total = before + (i - start) * per
            yield i
        self.total = before + (end - start) * per


def layer(nc, x, w_in, b_glu, conv_w, conv_b, conv_ln_g, conv_ln_b, lq1, lk1, lq2, lk2, subln_g,
          rel_bias, w_out, ln1_g, ln1_b, peer_wq, peer_keys, peer_u, peer_v, ln2_g, ln2_b, out):
    bias_rows = nc.dram_tensor("bias_rows", [HEADS, BV], F32, kind="Internal")
    gates = nc.dram_tensor("gates", [NK, NK, T], F32, kind="Internal")
    acts = nc.dram_tensor("acts", [NK, NK, T], F32, kind="Internal")
    scores_d = nc.dram_tensor("scores", [TT, P, HC * NK], F32, kind="Internal")
    resid = nc.dram_tensor("resid", [TT, P, D], F32, kind="Internal")

    top = [16512]

    def place(name, shape, dt, at=None):
        size = int(np.prod(shape[1:])) * {F32: 4, F32R: 4, BF16: 2, U32: 4}[dt]
        if at is None:
            at = top[0]
            top[0] += (size + 31) // 32 * 32
        return nc.alloc_sbuf_tensor_at(name, shape, dt, offset=at), at, at + size

    def fixed(name, shape, dt):
        return place(name, shape, dt)[0]

    actT = fixed("actT", [P, 2, KT, T], F32R)
    raw, RAW, _ = place("raw", [P, 2, PIECES, CB], F32)
    hl, HL, _ = place("hl", [P, PIECES, 2, CB], F32R)
    acc, ACC, _ = place("acc", [P, TT, D], F32)
    ident = fixed("ident", [P, P], F32)
    ones = fixed("ones", [P, P], F32)
    iota_row = fixed("iota_row", [P, P], BF16)
    iota_top = fixed("iota_top", [P, TOPK], F32)
    chan = fixed("chan", [P, CT, TAPS + 5], F32)
    sub_g = fixed("sub_g", [P, 1], F32)
    lam_in = fixed("lam_in", [P, 4, DH], F32)
    lam_pr = fixed("lam_pr", [P, 2, DH], F32)
    lam_s = fixed("lam_s", [P, 2], F32)
    map_scale = fixed("map_scale", [P, 2], F32)
    neg_lam = fixed("neg_lam", [P, 1], F32)
    neg_max = fixed("neg_max", [P, 2, 2], F32)
    esum = fixed("esum", [P, 2, 2], F32)
    rsum = fixed("rsum", [P, 2, 2], F32)
    ms = fixed("ms", [P, HEADS * TT], F32)
    ln_stats = fixed("ln_stats", [P, TT, 4, 6], F32)
    ln_mv = fixed("ln_mv", [P, TT, 2], F32)
    ln_rstd = fixed("ln_rstd", [P, TT, 1], F32)
    ln_shift = fixed("ln_shift", [P, TT, 1], F32)
    X = top[0]
    END = 229344

    def region(name, shape, dt, at):
        h, _, end = place(name, shape, dt, at)
        assert end <= END, (name, end - END)
        return h, (end + 31) // 32 * 32

    xrow, _ = region("xrow", [P, TT, D], F32, ACC)
    conv_y, e_ = region("conv_y", [P, CT, T], F32, ACC)
    conv_in, _ = region("conv_in", [P, 4, TAPS - 1 + T], F32, e_)
    conv_sq, _ = region("conv_sq", [P, CT, T], F32, e_)
    qk, e_ = region("qk", [P, 2 * HEADS, T], F32, X)
    vN, e_ = region("vN", [P, TT, HEADS * P], F32, e_)
    bias_t, m1 = region("bias_t", [P, 2, T], F32, e_)
    ex, m2 = region("ex", [P, 2, 2, T], F32, m1)
    pT, m3 = region("pT", [P, 2, T], F32, m2)
    qz, m4 = region("qz", [P, 2, T], F32, m3)
    sig, _ = region("sig", [P, 4, T], F32, m1)
    conv_mu, _ = region("conv_mu", [P, T], F32, m2)
    conv_std, _ = region("conv_std", [P, T], F32, m2 + 2048)
    junk, _ = region("junk", [P, TT, P], F32, m4)
    rows, _ = region("rows", [TAPS + 5, DC], F32, m3)
    rel_t, m5 = region("rel_t", [HEADS, BUCKETS], F32, e_)
    bv, _ = region("bv", [HEADS, BV], F32, m5)
    gb1, _ = region("gb1", [P, 2, D], F32, X + 2 * HEADS * T * 4)
    qp, e_ = region("qp", [P, HC, T], F32, X)
    keysT, e_ = region("keysT", [P, HC, NK], F32, e_)
    keys_in, _ = region("keys_in", [P, HC, NK], F32, X + 62464)
    sc_all, _ = region("sc_all", [P, TT, HC * NK], F32, ACC)
    sc, e_ = region("sc", [P, HC, NK], F32, ACC)
    cand, _ = region("cand", [P, PH, TOPK * TOPK], F32, ACC)
    pick_u, m1 = region("pick_u", [P, 2, PH, TOPK], U32, ACC)
    pick_f, m1 = region("pick_f", [P, 2, PH, TOPK], F32, m1)
    top_f, _ = region("top_f", [P, HC, TOPK], F32, m1)
    sc2, e_ = region("sc2", [P, HC, NK], F32, e_)
    hot_j, e_ = region("hot_j", [P, 2, 4, NK], F32R, e_)
    hot_i, _ = region("hot_i", [P, 2, 4, 2, NK], F32R, ACC + HC * NK * 4)
    gate_hl, e_ = region("gate_hl", [P, 2, P], F32R, e_)
    top_v, e_ = region("top_v", [P, HC, TOPK], F32, e_)
    top_i, e_ = region("top_i", [P, HC, TOPK], U32, e_)
    best_v, e_ = region("best_v", [P, PH, TOPK], F32, e_)
    best_c, e_ = region("best_c", [P, PH, TOPK], U32, e_)
    ij, e_ = region("ij", [P, 3, PH * TOPK], F32, e_)
    picks, e_ = region("picks", [P, 3, P], F32, e_)
    gsum, e_ = region("gsum", [P, 2, PH], F32, e_)
    table_lo, e_ = region("table_lo", [P, 2, 4, NK], F32, e_)
    assert e_ <= ACC + TT * D * 4
    gbuf, e_ = region("gbuf", [P, NK, P], F32, X)
    act_o, e_ = region("act_o", [P, 2, T], F32, e_)
    ut_raw_s, e_ = region("ut_raw_s", [P, 2, 4, P], F32, e_)
    u_in, _ = region("u_in", [P, 2, D], F32, RAW)
    utT, _ = region("utT", [P, 4, 2, 4, P], F32R, HL)
    raw_v, e_ = region("raw_v", [P, 2, PIECES, CB], F32, X)
    gb2, _ = region("gb2", [P, 2, D], F32, X)
    hl_v, e_ = region("hl_v", [P, PIECES, 2, CB], F32R, e_)
    w_hl, e_ = region("w_hl", [P, 4, 2, T], F32R, e_)
    act_in, e_ = region("act_in", [P, 4, T], F32, e_)
    gate_in, e_ = region("gate_in", [P, 4, T], F32, e_)
    assert e_ <= X + NK * P * 4
    ctx = ExitStack()
    with ctx:
        psum = ctx.enter_context(nc.psum_tensor("psum", [P, 8, CB], F32))

        def sem(name):
            return ctx.enter_context(nc.semaphore(name))

        x_in = [sem(f"x_in{t}") for t in range(TT)]
        par_in = sem("par_in")
        consts = sem("consts")
        bv_built = sem("bv_built")
        bias_out = sem("bias_out")
        chan_t = sem("chan_t")
        chan_ok = sem("chan_ok")
        lam_step = sem("lam_step")
        lam_exp = sem("lam_exp")
        raw_in = [sem(f"raw_in{s}") for s in range(2)]
        piece_hi = sem("piece_hi")
        piece_lo = sem("piece_lo")
        piece_used = sem("piece_used")
        half_done = sem("half_done")
        bank_done = sem("bank_done")
        tr_ps = sem("tr_ps")
        tr_hi = sem("tr_hi")
        tr_lo = sem("tr_lo")
        sig_ok = sem("sig_ok")
        glu_ok = sem("glu_ok")
        conv_pad = sem("conv_pad")
        conv_step = sem("conv_step")
        cl_sum = sem("cl_sum")
        cl_mu = sem("cl_mu")
        cl_sub = sem("cl_sub")
        cl_sq = sem("cl_sq")
        cl_var = sem("cl_var")
        cl_std = sem("cl_std")
        cl_rstd = sem("cl_rstd")
        cl_mul = sem("cl_mul")
        cl_act = sem("cl_act")
        cl_hi = sem("cl_hi")
        cl_lo = sem("cl_lo")
        qk_ok = sem("qk_ok")
        v_ok = sem("v_ok")
        bias_in = [sem(f"bias_in{s}") for s in range(2)]
        qz_ok = sem("qz_ok")
        at_log = sem("at_log")
        at_add = sem("at_add")
        at_max = sem("at_max")
        at_exp = sem("at_exp")
        at_rz = sem("at_rz")
        at_rl = sem("at_rl")
        at_e1 = sem("at_e1")
        at_p = sem("at_p")
        at_tr = sem("at_tr")
        at_pt = sem("at_pt")
        at_pv = sem("at_pv")
        at_o = sem("at_o")
        fin_std = sem("fin_std")
        fin_r = sem("fin_r")
        fin_n = sem("fin_n")
        fin_t = sem("fin_t")
        fin_hi = sem("fin_hi")
        fin_lo = sem("fin_lo")
        x_again = sem("x_again")
        gb_in = sem("gb_in")
        out_ok = sem("out_ok")
        ln_stat = sem("ln_stat")
        ln_std = sem("ln_std")
        ln_r = sem("ln_r")
        ln_c = sem("ln_c")
        ln_y = sem("ln_y")
        ln_z = sem("ln_z")
        ln_zg = sem("ln_zg")
        ln_yp = sem("ln_yp")
        acc_ok = sem("acc_ok")
        keys_ld = sem("keys_ld")
        keys_t = sem("keys_t")
        keys_ok = sem("keys_ok")
        qp_ok = sem("qp_ok")
        sc_ps = sem("sc_ps")
        sc_ok = sem("sc_ok")
        rt = sem("rt")
        g_exp = sem("g_exp")
        pick_t = sem("pick_t")
        hot_ok = sem("hot_ok")
        g_mm = sem("g_mm")
        table_lo_ok = sem("table_lo_ok")
        g_ev = sem("g_ev")
        g_out = [sem(f"g_out{r}") for r in range(4)]
        act_st = [sem(f"act_st{s}") for s in range(2)]
        act_ld = [sem(f"act_ld{s}") for s in range(4)]
        sc_st = sem("sc_st")
        sc_in = sem("sc_in")
        res_st = sem("res_st")
        res_in = sem("res_in")
        u_ld = [sem(f"u_ld{s}") for s in range(2)]
        g_ld = [sem(f"g_ld{s}") for s in range(4)]
        ut_ps = sem("ut_ps")
        ut_hi = sem("ut_hi")
        ut_raw = sem("ut_raw")
        ut_lo = sem("ut_lo")
        ut_used = sem("ut_used")
        gelu_ok = sem("gelu_ok")
        w_made = sem("w_made")
        w_hi = sem("w_hi")
        w_lo = sem("w_lo")
        v_ready = sem("v_ready")
        v_added = sem("v_added")
        ln2_in = sem("ln2_in")
        y_out = sem("y_out")

        RT_STEPS = 138
        PARAMS = 11 * 16
        PRODUCTS = ((0, 0), (0, 1), (1, 0))

        def wait_bank(eng, b, c):
            if c < 3:
                before = B_WQ - B_OUT if isinstance(b, int) and b >= B_WQ else 0
                eng.wait_ge(bank_done, b * 3 + (c + 1 - 3 * before))
            else:
                eng.wait_ge(piece_used, b * KT + (KT + PIECES))

        def wait_half(eng, hb, c):
            if c < 3:
                eng.wait_ge(half_done, hb * 3 + (c + 1))
            else:
                eng.wait_ge(piece_used, hb * HK + (B_OUT * KT + HK + PIECES))

        block = ctx.enter_context(nc.Block())

        @block.sync
        def _(sp):
            for tt in range(TT):
                sp.dma_start(xrow[:, tt, :], x[0, tt * P:(tt + 1) * P, :]).then_inc(x_in[tt], 16)

            def load(n, slot, w, row, col, dst=raw):
                if not (isinstance(n, int) and n < 2):
                    sp.wait_ge(piece_lo, n * PIECES - PIECES)
                src = w[0, bass.ds(row, PIECES * P), bass.ds(col, CB)]
                sp.dma_start(dst[:, slot, :, :], src.rearrange("(j p) c -> p j c", p=P)).then_inc(raw_in[slot], 16)

            def load_block(b, w, col, r0=0):
                for r in range(r0, LOADS):
                    load(b * LOADS + r, r % 2, w, r * PIECES * P, col)

            glu_col = [GLU_COL0 + DC, GLU_COL0, GLU_COL0 + DC + CB, GLU_COL0 + CB]
            load(0, 0, w_in, 0, glu_col[0])
            sp.dma_start(rows[0:TAPS, :], conv_w[0]).then_inc(par_in, 16)
            sp.dma_start(rows[TAPS:TAPS + 1, :], conv_b).then_inc(par_in, 16)
            sp.dma_start(rows[TAPS + 1:TAPS + 2, :], conv_ln_g).then_inc(par_in, 16)
            sp.dma_start(rows[TAPS + 2:TAPS + 3, :], conv_ln_b).then_inc(par_in, 16)
            sp.dma_start(rows[TAPS + 3:TAPS + 5, :], b_glu.rearrange("a (g c) -> (a g) c", g=2)).then_inc(par_in, 16)
            sp.dma_start(sub_g[:, :], subln_g.rearrange("a p -> p a")).then_inc(par_in, 16)
            for n, v in enumerate((lq1, lk1, lq2, lk2)):
                sp.dma_start(lam_in[:, n, :], bass.AP(v.tensor, v.offset, [[0, P], [1, DH]])).then_inc(par_in, 16)
            sp.dma_start(rel_t[:, :], rel_bias.rearrange("b h -> h b"), allow_slow_non_contiguous=True).then_inc(par_in, 16)
            load(1, 1, w_in, PIECES * P, glu_col[0])
            sp.wait_ge(bv_built, 1)
            sp.dma_start(bias_rows.ap(), bv[:, :]).then_inc(bias_out, 16)
            load_block(0, w_in, glu_col[0], 2)
            for b in range(1, B_QK):
                load_block(b, w_in, glu_col[b])
            sp.wait_ge(bias_out, 16)

            def load_bias(h, slot):
                sp.dma_start(bias_t[:, slot, :],
                             bass.AP(bias_rows, h * BV, [[1, P], [1, T]])).then_inc(bias_in[slot], 16)

            for h in range(2):
                load_bias(h, h)
            with sp.Fori(0, 4) as i:
                load_block(i + B_QK, w_in, i * CB)
            with sp.Fori(0, 2) as i:
                load_block(i + B_V, w_in, i * CB + V_COL0)

            def load_out(hb, half, row, col):
                load(hb * HALF_LOADS + (B_OUT * LOADS + half), half, w_out, row + half * PIECES * P, col)

            for half in range(2):
                load_out(0, half, HK * P, 0)
            sp.wait_ge(cl_lo, CT)
            for tt in range(TT):
                sp.dma_start(acc[:, tt, :], x[0, tt * P:(tt + 1) * P, :]).then_inc(x_again, 16)
            with sp.Fori(0, HEADS // 2 - 1) as i:
                for hh in range(2):
                    load_out(i + 1, hh, HK * P, (i + 1) * CB)
                    sp.wait_ge(at_add, i * 8 + (4 * hh + 4))
                    load_bias(i * 2 + (hh + 2), hh)
            for hb in range(4, 6):
                for half in range(2):
                    load_out(hb, half, 0, (hb - 4) * CB)
            sp.wait_ge(at_pv, HEADS * TT + 2)
            for n, v in enumerate((ln1_g, ln1_b)):
                sp.dma_start(gb1[:, n, :], bass.AP(v.tensor, v.offset, [[0, P], [1, D]])).then_inc(gb_in, 16)
            with sp.Fori(2, 4) as i:
                for half in range(2):
                    load_out(i + 4, half, 0, i * CB)
            sp.wait_ge(fin_lo, HEADS)
            sp.dma_start(keys_in[:, :, :], peer_keys[0].rearrange("h c n d -> n (h c) d")).then_inc(keys_ld, 16)
            load_block(B_WQ, peer_wq, 0)
            load_block(B_WQ + 1, peer_wq, CB)
            for tt in range(TT):
                sp.wait_ge(acc_ok, tt + 1)
                sp.dma_start(resid.ap()[tt], acc[:, tt, :]).then_inc(res_st, 16)
            load_block(B_WQ + 2, peer_wq, 2 * CB)
            load_block(B_WQ + 3, peer_wq, 3 * CB)

            def load_u(n, slot):
                if not (isinstance(n, int) and n < 2):
                    sp.wait_ge(ut_ps, n * 4 - 4)
                sp.dma_start(u_in[:, slot, :], peer_u[0, bass.ds(n * P, P), :]).then_inc(u_ld[slot], 16)

            sp.wait_ge(piece_lo, BLOCKS * KT)
            load_u(0, 0)
            load_u(1, 1)
            for tt in range(TT):
                sp.wait_ge(sc_ok, 4 * tt + 4)
                sp.dma_start(scores_d.ap()[tt], sc_all[:, tt, :]).then_inc(sc_st, 16)
            sp.wait_ge(sc_st, TT * 16)

            def load_scores(tt):
                sp.dma_start(sc[:, :, :].rearrange("p h n -> p (h n)"), scores_d.ap()[tt]).then_inc(sc_in, 16)

            def store_acts(n, slot):
                sp.wait_ge(gelu_ok, n + 3)
                sp.dma_start(acts.ap()[bass.ds(n, 1), :, :].rearrange("a j t -> j (a t)"), act_o[:, slot, :]
                             ).then_inc(act_st[slot], 16)

            def load_weights(m, c):
                sp.wait_ge(w_made, m + 1)
                sp.dma_start(gate_in[:, c, :], gates.ap()[bass.ds(m, 1), :, :].rearrange("a j t -> j (a t)")
                             ).then_inc(g_ld[c], 16)
                sp.wait_ge(w_lo, m + 1)
                sp.wait_ge(act_st[c % 2], (m - (c % 2)) * 8 + 32)
                sp.dma_start(act_in[:, c, :], acts.ap()[bass.ds(m, 1), :, :].rearrange("a j t -> j (a t)")
                             ).then_inc(act_ld[c], 16)

            def load_v(g, c):
                load((g + BLOCKS) * LOADS + c, c % 2, peer_v, g * (PIECES * P), c * CB, raw_v)

            for s in range(2):
                sp.sem_inc(act_st[s], 16)
            load_scores(0)
            def chunk_io(n0, count, stored=None):
                first = 0
                if stored is not None:
                    first = 4
                    sp.wait_ge(g_ev, 32 * (stored + 1) + 2)
                    for n, r in enumerate((0, 3, 1, 2)):
                        load_u(n0 + n + 2, n % 2)
                        i4 = slice(r * NK // 4, (r + 1) * NK // 4)
                        sp.dma_start(gates.ap().rearrange("i j t -> j i t")[:, i4, stored * P:(stored + 1) * P],
                                     gbuf[:, i4, :]).then_inc(g_out[r], 16)
                        store_acts(n0 + n, n % 2)
                if first == count:
                    return
                with sp.Fori(first // 2, count // 2) as i:
                    for c in range(2):
                        load_u(i * 2 + (n0 + c + 2), c)
                        store_acts(i * 2 + (n0 + c), c)

            n0 = 0
            for tt in range(TT):
                chunk_io(n0, ROUTE_CHUNKS, tt - 1 if tt else None)
                n0 += ROUTE_CHUNKS
                if tt + 1 < TT:
                    sp.wait_ge(rt, RT_STEPS * (tt + 1))
                    load_scores(tt + 1)
                chunk_io(n0, GATE_CHUNKS)
                n0 += GATE_CHUNKS
            chunk_io(n0, 4, TT - 1)
            sp.wait_ge(g_out[0], TT * 16)
            load_v(0, 0)
            load_v(0, 1)
            sp.wait_ge(g_out[3], TT * 16)
            for c in range(4):
                load_weights(c, c)
            chunk_io(n0 + 4, STORE_CHUNKS - 4)
            assert n0 + STORE_CHUNKS == AHEAD
            for tt in range(TT):
                sp.dma_start(acc[:, tt, :], resid.ap()[tt]).then_inc(res_in, 16)
            for r in range(1, 3):
                sp.wait_ge(g_out[r], TT * 16)

            def group_loads(g, with_u, last_u, last):
                for c in range(4):
                    if c < 2:
                        load_v(g, c + 2)
                    elif not last:
                        load_v(g + 1, c - 2)
                    if not last:
                        load_weights(g * 4 + (4 + c), c)
                    n = g * 4 + (AHEAD + c)
                    if with_u:
                        if not (last_u and c >= 2):
                            load_u(n + 2, c % 2)
                        store_acts(n, c % 2)

            with sp.Fori(0, GROUPS - AHEAD_GROUPS - 1) as g:
                group_loads(g, True, False, False)
            group_loads(GROUPS - AHEAD_GROUPS - 1, True, True, False)
            with sp.Fori(GROUPS - AHEAD_GROUPS, GROUPS - 1) as g:
                group_loads(g, False, False, False)
            group_loads(GROUPS - 1, False, False, True)
            sp.wait_ge(piece_lo, (BLOCKS + GROUPS) * KT)
            for n, v in enumerate((ln2_g, ln2_b)):
                sp.dma_start(gb2[:, n, :], bass.AP(v.tensor, v.offset, [[0, P], [1, D]])).then_inc(ln2_in, 16)
            for tt in range(TT):
                sp.wait_ge(ln_y, TT + tt + 1)
                sp.wait_ge(ln_yp, TT + tt + 1)
                sp.dma_start(out[0, tt * P:(tt + 1) * P, :], acc[:, tt, :]).then_inc(y_out, 16)
            sp.wait_ge(y_out, TT * 16)
            for s in range(2):
                sp.wait_ge(act_st[s], NK // 2 * 16 + 16)

        @block.gpsimd
        def _(pool):
            pool.sem_inc(w_lo, 4)
            nc.gpsimd.memset(ident[:, :], 0.0).then_inc(consts, 1)
            nc.gpsimd.memset(ones[:, :], 1.0).then_inc(consts, 1)
            nc.gpsimd.iota(iota_row[:, :], pattern=[[1, P]], base=0, channel_multiplier=0,
                           allow_small_or_imprecise_dtypes=True).then_inc(consts, 1)
            nc.gpsimd.iota(iota_top[:, :], pattern=[[1, TOPK]], base=0, channel_multiplier=0,
                           allow_small_or_imprecise_dtypes=True).then_inc(consts, 1)
            nc.gpsimd.memset(map_scale[:, :], DH ** -0.5).then_inc(consts, 1)
            pool.wait_ge(consts, 5)
            nc.gpsimd.affine_select(out=ident[:, :], in_=ident[:, :], compare_op=ALU.not_equal, fill=1.0,
                                    base=0, pattern=[[-1, P]], channel_multiplier=1).then_inc(consts, 1)
            nc.gpsimd.affine_select(out=map_scale[:, 0:1], in_=map_scale[:, 0:1], compare_op=ALU.is_gt, fill=0.0,
                                    base=DH, pattern=[[0, 1]], channel_multiplier=-1).then_inc(consts, 1)
            nc.gpsimd.affine_select(out=map_scale[:, 1:2], in_=map_scale[:, 1:2], compare_op=ALU.is_ge, fill=0.0,
                                    base=-DH, pattern=[[0, 1]], channel_multiplier=1).then_inc(consts, 1)
            pool.wait_ge(consts, 8)

            def lows(p, k0, k1, raw=raw, hl=hl):
                for k in range(k0, k1):
                    slot = k % PIECES
                    pool.wait_ge(piece_hi, p + (k + 1))
                    nc.gpsimd.tensor_tensor(hl[:, slot, 1, :], raw[:, k // PIECES % 2, slot, :],
                                            hl[:, slot, 0, :].bitcast(F32), ALU.subtract).then_inc(piece_lo, 1)

            lows(0, 0, PIECES)
            def masked_q(h):
                for m in range(2):
                    nc.gpsimd.tensor_tensor(qz[:, m, :], qk[:, bass.ds(h, 1), :].rearrange("p a t -> p (a t)"),
                                            bass.AP(map_scale, m, [[2, P], [0, T]]), ALU.mult).then_inc(qz_ok, 1)

            with pool.Fori(0, B_V + 1) as b:
                lows(b * KT, PIECES, KT + PIECES)
            pool.wait_ge(qk_ok, 4 * 4 + 8)
            masked_q(0)
            lows((B_V + 1) * KT, PIECES, KT + PIECES)
            for ct in range(CT):
                pool.wait_ge(cl_hi, ct + 1)
                nc.gpsimd.tensor_tensor(actT[:, 1, CT + ct, :], conv_y[:, ct, :],
                                        actT[:, 0, CT + ct, :].bitcast(F32), ALU.subtract).then_inc(cl_lo, 1)

            def two_heads(i, last):
                p = i * HK + B_OUT * KT
                lows(p, 4, 6)
                pool.wait_ge(at_log, i * 8 + (4 + 4))
                masked_q(i * 2 + 1)
                lows(p, 6, 9)
                if not last:
                    pool.wait_ge(at_log, i * 8 + (8 + 4))
                    masked_q(i * 2 + 2)
                lows(p, 9, 12)

            with pool.Fori(0, HEADS // 2 - 1) as i:
                two_heads(i, False)
            two_heads(HEADS // 2 - 1, True)
            with pool.Fori(4, 8) as hb:
                lows(hb * HK + B_OUT * KT, PIECES, HK + PIECES)

            def gamma_beta(which, gb, gb_sem):
                pool.wait_ge(gb_sem, 32)
                for tt in range(TT):
                    pool.wait_ge(ln_z, TT * which + tt + 1)
                    a = acc[:, tt, LN_DVE:D]
                    nc.gpsimd.tensor_tensor(a, a, gb[:, 0, LN_DVE:D], ALU.mult).then_inc(ln_zg, 1)
                    pool.wait_ge(ln_zg, TT * which + tt + 1)
                    nc.gpsimd.tensor_tensor(a, a, gb[:, 1, LN_DVE:D], ALU.add).then_inc(ln_yp, 1)

            gamma_beta(0, gb1, gb_in)
            with pool.Fori(B_WQ, BLOCKS - 1) as b:
                lows(b * KT, PIECES, KT + PIECES)
            lows((BLOCKS - 1) * KT, PIECES, KT)

            def u_low(n, kq):
                pool.wait_ge(ut_raw, n * 4 + (kq + 3))
                nc.gpsimd.tensor_tensor(utT[:, kq, 1, :, :], ut_raw_s[:, kq % 2, :, :],
                                        utT[:, kq, 0, :, :].bitcast(F32), ALU.subtract).then_inc(ut_lo, 1)

            with pool.Fori(0, AHEAD) as n:
                for kq in range(4):
                    u_low(n, kq)

            def weight_lows(n, c):
                pool.wait_ge(w_hi, n + 1)
                nc.gpsimd.tensor_tensor(w_hl[:, c, 1, :], act_in[:, c, :], w_hl[:, c, 0, :].bitcast(F32),
                                        ALU.subtract).then_inc(w_lo, 1)

            lows(BLOCKS * KT, 0, PIECES, raw_v, hl_v)
            for c in range(4):
                weight_lows(c, c)
            with pool.Fori(0, GROUPS - 1) as g:
                lows((g + BLOCKS) * KT, PIECES, KT, raw_v, hl_v)
                for c in range(4):
                    lows((g + BLOCKS) * KT, KT + c, KT + c + 1, raw_v, hl_v)
                    weight_lows(g * 4 + (4 + c), c)
            lows((BLOCKS + GROUPS - 1) * KT, PIECES, KT, raw_v, hl_v)
            gamma_beta(1, gb2, ln2_in)

        @block.scalar
        def _(act):
            def highs(p, loaded, k0, k1, raw=raw, hl=hl):
                for k in range(k0, k1):
                    slot, rs = k % PIECES, k // PIECES % 2
                    if slot == 0:
                        act.wait_ge(raw_in[rs], loaded + 16 * (k // PIECES // 2 + 1))
                    act.wait_ge(piece_used, p + (k + 1))
                    nc.scalar.activation(hl[:, slot, 0, :], raw[:, rs, slot, :], ACT.Copy).then_inc(piece_hi, 1)

            def block_highs(b, k0=PIECES, k1=KT + PIECES, raw=raw, hl=hl):
                highs(b * KT, b * (LOADS // 2 * 16), k0, k1, raw, hl)

            def half_highs(hb, k0, k1):
                highs(hb * HK + B_OUT * KT, hb * 16 + B_OUT * (LOADS // 2 * 16), k0, k1)

            act.sem_inc(sig_ok, 4)
            act.sem_inc(at_o, 1)
            act.sem_inc(qk_ok, 8)
            act.sem_inc(qp_ok, 8)
            act.sem_inc(gelu_ok, 2)

            def transposed_highs(base):
                for u in range(TT * 4):
                    tt, kq = u // 4, u % 4
                    act.wait_ge(tr_ps, base + u + 1)
                    nc.scalar.activation(actT[:, 0, 4 * kq:4 * kq + 4, tt * P:(tt + 1) * P],
                                         psum[:, u % 4, :].rearrange("p (k t) -> p k t", k=4),
                                         ACT.Copy).then_inc(tr_hi, 1)

            transposed_highs(0)
            block_highs(0, 0, PIECES)
            act.wait_ge(chan_t, 1)
            nc.scalar.activation(chan[:, :, :], psum[:, 7, 0:CT * (TAPS + 5)].rearrange("p (c r) -> p c r", c=CT),
                                 ACT.Copy).then_inc(chan_ok, 1)
            act.wait_ge(lam_step, 2)
            nc.scalar.activation(lam_s[:, :], lam_s[:, :], ACT.Exp).then_inc(lam_exp, 1)

            act.wait_ge(chan_ok, 1)
            with act.Fori(0, 2) as j:
                block_highs(j * 2)
                act.wait_ge(glu_ok, j * 4 + 4)
                for c in range(4):
                    wait_bank(act, j * 2, c)
                    nc.scalar.activation(sig[:, c, :], psum[:, c, :], ACT.Sigmoid,
                                         bias=chan[:, bass.ds(j * 4 + c, 1), TAPS + 4:TAPS + 5].rearrange("p a b -> p (a b)")
                                         ).then_inc(sig_ok, 1)
                block_highs(j * 2 + 1)
            with act.Fori(0, 2) as i:
                for half in range(2):
                    block_highs(i * 2 + (B_QK + half))
                    for c in range(4):
                        wait_bank(act, i * 2 + (B_QK + half), c)
                        nc.scalar.activation(qk[:, bass.ds(i * 8 + (4 * half + c), 1), :].rearrange("p a t -> p (a t)"),
                                             psum[:, 4 * half + c, :], ACT.Copy).then_inc(qk_ok, 1)
            act.wait_ge(cl_sum, 1)
            nc.scalar.activation(conv_mu[:, :], psum[:, 0, :], ACT.Copy, scale=1.0 / DC).then_inc(cl_mu, 1)
            for ct in range(CT):
                act.wait_ge(cl_sub, ct + 1)
                nc.scalar.activation(conv_sq[:, ct, :], conv_y[:, ct, :], ACT.Square).then_inc(cl_sq, 1)
            for half in range(2):
                block_highs(B_V + half)
                if half == 0:
                    for c in range(4):
                        wait_bank(act, B_V, c)
                        nc.scalar.activation(vN[:, c, 0:CB], psum[:, c, :], ACT.Copy).then_inc(v_ok, 1)
                    act.wait_ge(cl_var, 1)
                    nc.scalar.activation(conv_std[:, :], psum[:, 4, :], ACT.Sqrt, scale=1.0 / DC, bias=EPS
                                         ).then_inc(cl_std, 1)
                    for ct in range(CT):
                        act.wait_ge(cl_mul, ct + 1)
                        nc.scalar.activation(conv_y[:, ct, :], conv_y[:, ct, :], ACT.Silu,
                                             scale=chan[:, ct, TAPS + 1:TAPS + 2], bias=chan[:, ct, TAPS + 2:TAPS + 3]
                                             ).then_inc(cl_act, 1)
            act.wait_ge(cl_act, CT)

            def conv_highs(c0, c1):
                for ct in range(c0, c1):
                    nc.scalar.activation(actT[:, 0, CT + ct, :], conv_y[:, ct, :], ACT.Copy).then_inc(cl_hi, 1)

            for c in range(4):
                wait_bank(act, B_V + 1, c)
                if c == 3:
                    conv_highs(0, 1)
                nc.scalar.activation(vN[:, c, CB:2 * CB], psum[:, 4 + c, :], ACT.Copy).then_inc(v_ok, 1)

            def exps(s, t):
                act.wait_ge(at_max, s + 1)
                for m in range(2):
                    e = ex[:, t % 2, m, 0:(t + 1) * P]
                    nc.scalar.activation(e, e, ACT.Exp, bias=neg_max[:, t % 2, m:m + 1],
                                         accum_out=esum[:, t % 2, m:m + 1]).then_inc(at_exp, 1)

            def keep_head(h):
                act.wait_ge(at_pv, h * TT + (TT + 2))
                act.wait_ge(at_o, h + 1)
                o = qk[:, bass.ds(h, 1), :].rearrange("p a t -> p (a t)")
                nc.scalar.activation(o, psum[:, 3, :], ACT.Copy)
                for t in range(TT):
                    last = nc.scalar.activation(junk[:, t, :], psum[:, 3, t * P:(t + 1) * P], ACT.Square,
                                                accum_out=ms[:, bass.ds(h * TT + t, 1)])
                last.then_inc(at_o, 1)

            def attention_heads(i, last):
                piece = PIECES
                for k in range(2 * TT):
                    s, t = i * (2 * TT) + k, k % TT
                    if not (last and k == 2 * TT - 1):
                        exps(s + 1, (t + 1) % TT)
                    act.wait_ge(at_tr, s + 2)
                    act.wait_ge(at_pv, s + 1)
                    nc.scalar.activation(pT[:, t % 2, 0:(t + 1) * P], psum[:, 2, 0:(t + 1) * P],
                                         ACT.Copy).then_inc(at_pt, 1)
                    if k == TT:
                        keep_head(i * 2)
                    half_highs(i, piece, piece + FILL[k])
                    piece += FILL[k]
                keep_head(i * 2 + 1)
                half_highs(i, piece, HK + PIECES)

            conv_highs(1, 3)
            exps(0, 0)
            conv_highs(3, CT)
            with act.Fori(0, HEADS // 2 - 1) as i:
                attention_heads(i, False)
            attention_heads(HEADS // 2 - 1, True)
            act.wait_ge(at_o, HEADS + 1)
            nc.scalar.activation(ms[:, :], ms[:, :], ACT.Sqrt, scale=1.0 / P, bias=EPS).then_inc(fin_std, 1)
            for h in range(HEADS):
                act.wait_ge(fin_t, h + 1)
                nc.scalar.activation(actT[:, 0, h, :], psum[:, h % 4, :], ACT.Copy, scale=sub_g[:, 0:1]
                                     ).then_inc(fin_hi, 1)
                if h >= 4:
                    half_highs(4, h, h + 1)
            half_highs(4, HK, HK + PIECES)
            with act.Fori(5, 8) as hb:
                half_highs(hb, PIECES, HK + PIECES)
            def centre(which):
                act.wait_ge(ln_stat, 20 * which + 20)
                nc.scalar.activation(ln_rstd[:, :, :], ln_mv[:, :, 1:2], ACT.Sqrt, bias=EPS).then_inc(ln_std, 1)
                act.wait_ge(ln_r, 2 * which + 2)
                for tt in range(TT):
                    a = acc[:, tt, LN_DVE:D]
                    nc.scalar.activation(a, a, ACT.Identity, scale=ln_rstd[:, tt, :], bias=ln_shift[:, tt, :]).then_inc(ln_z, 1)

            centre(0)
            transposed_highs(16)
            for tt in range(TT):
                nc.scalar.activation(acc[:, tt, :], acc[:, tt, :], ACT.Copy, scale=ALPHA).then_inc(acc_ok, 1)
            for r in range(4):
                act.wait_ge(keys_t, r + 1)
                nc.scalar.activation(keysT[:, 4 * r:4 * r + 4, :], psum[:, 4 + r, :].rearrange("p (k n) -> p k n", k=4),
                                     ACT.Copy).then_inc(keys_ok, 1)
            for b in range(B_WQ, BLOCKS):
                half = b % 2
                block_highs(b, PIECES, KT + PIECES if b + 1 < BLOCKS else KT)
                for c in range(4):
                    wait_bank(act, b, c)
                    nc.scalar.activation(qp[:, 4 * (b - B_WQ) + c, :], psum[:, 4 * half + c, :], ACT.Copy).then_inc(qp_ok, 1)
            act.wait_ge(res_st, TT * 16)
            for tt in range(TT):
                for r in range(4):
                    act.wait_ge(sc_ps, 4 * tt + r + 1)
                    nc.scalar.activation(sc_all[:, tt, 4 * r * NK:4 * (r + 1) * NK],
                                         psum[:, 4 * (tt % 2) + r, :], ACT.Copy).then_inc(sc_ok, 1)

            def u_high(n, kq, keep_raw):
                squares = psum[:, 4 + kq % 2, :].rearrange("p (k e) -> p k e", k=4)
                act.wait_ge(ut_ps, n * 4 + (kq + 1))
                act.wait_ge(ut_used, n * 4 + (kq + 1))
                nc.scalar.activation(utT[:, kq, 0, :, :], squares, ACT.Copy).then_inc(ut_hi, 1)
                if keep_raw:
                    act.wait_ge(ut_lo, n * 4 + (kq + 1))
                    nc.scalar.activation(ut_raw_s[:, kq % 2, :, :], squares, ACT.Copy).then_inc(ut_raw, 1)

            def gelu(n, c):
                act.wait_ge(ut_used, n * 4 + 8)
                act.wait_ge(act_st[c % 2], (n - (c % 2)) * 8 + 16)
                nc.scalar.activation(act_o[:, c % 2, :], psum[:, 6 + c % 2, :], ACT.Gelu).then_inc(gelu_ok, 1)

            def weight_highs(m, c):
                act.wait_ge(w_made, m + 5)
                if not (isinstance(m, int) and m < 4):
                    act.wait_ge(piece_used, m * 4 - 3 * c + (BLOCKS * KT - 16 + 12 + 1 + PIECES))
                nc.scalar.activation(w_hl[:, c, 0, :], act_in[:, c, :], ACT.Copy).then_inc(w_hi, 1)

            def keep_low_table(quad, tt, b):
                act.wait_ge(g_mm, quad * 4 + (tt * P + 12))
                act.wait_ge(g_ev, quad + (tt * 32 + 1))
                lo = psum[:, 2 * b:2 * b + 2, :].rearrange("p b (t h i) -> p (b t) h i", t=2, h=2)[:, :, 1, :]
                nc.scalar.activation(table_lo[:, b, :, :], lo, ACT.Copy).then_inc(table_lo_ok, 1)

            u_high(0, 0, True)
            u_high(0, 1, True)

            def plain_chunks(n0, count, last):
                def pair(i, end):
                    for c in range(2):
                        n = i * 2 + (n0 + c)
                        u_high(n, 2, True)
                        u_high(n, 3, True)
                        for kq in range(2):
                            u_high(n + 1, kq, not (end and c))
                        gelu(n, c)
                if last:
                    with act.Fori(0, count // 2 - 1) as i:
                        pair(i, False)
                    pair(count // 2 - 1, True)
                else:
                    with act.Fori(0, count // 2) as i:
                        pair(i, False)

            n0 = 0
            for tt in range(TT):
                plain_chunks(n0, ROUTE_CHUNKS - 2, False)
                act.wait_ge(rt, RT_STEPS * tt + 123)
                nc.scalar.activation(ij[:, 2, :], ij[:, 2, :], ACT.Exp).then_inc(g_exp, 1)
                plain_chunks(n0 + ROUTE_CHUNKS - 2, 2, False)
                n0 += ROUTE_CHUNKS
                with act.Fori(0, GATE_CHUNKS // 2) as i:
                    for c in range(2):
                        n = i * 2 + (n0 + c)
                        for part in range(4):
                            keep_low_table(i * (2 * QUADS) + (c * QUADS + part), tt, part % 2)
                            u_high(n + part // 2, (2 + part) % 4, True)
                        gelu(n, c)
                n0 += GATE_CHUNKS
            plain_chunks(n0, STORE_CHUNKS, True)
            act.wait_ge(g_out[1], TT * 16)
            block_highs(BLOCKS, 0, PIECES, raw_v, hl_v)
            act.wait_ge(g_out[2], TT * 16)
            for c in range(4):
                weight_highs(c, c)

            def expert_group(g, with_u, last_u):
                for c in range(4):
                    n = g * 4 + (AHEAD + c)
                    k0 = PIECES * c
                    if c:
                        block_highs(g + BLOCKS, k0, k0 + 1, raw_v, hl_v)
                    if with_u:
                        u_high(n, 2, False)
                    if c:
                        block_highs(g + BLOCKS, k0 + 1, k0 + 2, raw_v, hl_v)
                    if with_u:
                        u_high(n, 3, False)
                    if c:
                        block_highs(g + BLOCKS, k0 + 2, k0 + 4, raw_v, hl_v)
                    if with_u:
                        if not (last_u and c == 3):
                            u_high(n + 1, 0, False)
                            u_high(n + 1, 1, False)
                        gelu(n, c)
                for c in range(4):
                    block_highs(g + BLOCKS, KT + c, KT + c + 1, raw_v, hl_v)
                    weight_highs(g * 4 + (4 + c), c)

            with act.Fori(0, GROUPS - AHEAD_GROUPS - 1) as g:
                expert_group(g, True, False)
            expert_group(GROUPS - AHEAD_GROUPS - 1, True, True)
            with act.Fori(GROUPS - AHEAD_GROUPS, GROUPS - 1) as g:
                expert_group(g, False, False)
            block_highs(BLOCKS + GROUPS - 1, PIECES, KT, raw_v, hl_v)
            centre(1)

        @block.tensor
        def _(pe):
            pe.sem_inc(piece_used, PIECES)
            pe.sem_inc(at_tr, 1)
            pe.sem_inc(at_pv, 2)
            pe.sem_inc(at_log, 4)
            pe.sem_inc(g_mm, 8)
            pe.sem_inc(ut_used, 4)
            pe.wait_ge(consts, 8)
            def transposes(base, src, ready):
                for u in range(TT * 4):
                    tt, kq = u // 4, u % 4
                    if kq == 0:
                        ready(tt)
                    if base + u >= 4:
                        pe.wait_ge(tr_lo, base + u - 3)
                    for kk in range(4):
                        last = nc.tensor.transpose(psum[:, u % 4, kk * P:(kk + 1) * P],
                                                   src[:, tt, (4 * kq + kk) * P:(4 * kq + kk + 1) * P], ident[:, :])
                    last.then_inc(tr_ps, 1)

            transposes(0, xrow, lambda tt: pe.wait_ge(x_in[tt], 16))
            pe.wait_ge(par_in, PARAMS)
            for ct in range(CT):
                last = nc.tensor.transpose(psum[:, 7, ct * (TAPS + 5):(ct + 1) * (TAPS + 5)],
                                           rows[:, ct * P:(ct + 1) * P], ident[0:TAPS + 5, 0:TAPS + 5])
            last.then_inc(chan_t, 1)

            def column_block(b, first_bank, weights_stationary, transposed=0):
                for k in range(KT):
                    slot = k % PIECES
                    pe.wait_ge(piece_lo, b * KT + (k + 1))
                    for c in range(4):
                        if k == 0:
                            pe.wait_ge(tr_lo, transposed + 13 + c)
                        for n, (wi, ai) in enumerate(PRODUCTS):
                            w = hl[:, slot, wi, :]
                            a = actT[:, ai, k, :]
                            if weights_stationary:
                                lhsT, rhs = w[:, c * P:(c + 1) * P], a
                            else:
                                lhsT, rhs = a[:, c * P:(c + 1) * P], w
                            last = nc.tensor.matmul(psum[:, first_bank + c, :], lhsT, rhs,
                                                    start=(k == 0 and n == 0), stop=(k == KT - 1 and n == 2))
                        if k == KT - 1 and c < 3:
                            last.then_inc(bank_done, 1)
                    last.then_inc(piece_used, 1)

            def out_piece(hb, k, row_tile, first_bank):
                slot = k % PIECES
                pe.wait_ge(piece_lo, hb * HK + (B_OUT * KT + k + 1))
                for c in range(4):
                    for n, (wi, ai) in enumerate(PRODUCTS):
                        last = nc.tensor.matmul(psum[:, first_bank + c, :], actT[:, ai, row_tile, c * P:(c + 1) * P],
                                                hl[:, slot, wi, :], start=(k == 0 and n == 0), stop=(k == HK - 1 and n == 2))
                    if k == HK - 1 and c < 3:
                        last.then_inc(half_done, 1)
                last.then_inc(piece_used, 1)

            with pe.Fori(0, 2) as j:
                pe.wait_ge(sig_ok, j * 4 + 4)
                column_block(j * 2, 0, True)
                pe.wait_ge(glu_ok, j * 4 + 4)
                column_block(j * 2 + 1, 4, True)
            pe.wait_ge(sig_ok, 8 + 4)
            with pe.Fori(0, 2) as i:
                pe.wait_ge(qk_ok, i * 8 + 4)
                column_block(i * 2 + B_QK, 0, True)
                pe.wait_ge(glu_ok, 8 + 4)
                pe.wait_ge(qk_ok, i * 8 + 8)
                column_block(i * 2 + (B_QK + 1), 4, True)
            pe.wait_ge(conv_step, 2 * 4 * TAPS + 1)
            pe.wait_ge(qk_ok, 12 + 8)
            for ct in range(CT):
                last = nc.tensor.matmul(psum[:, 0, :], ones[:, :], conv_y[:, ct, :], start=ct == 0, stop=ct == CT - 1)
            last.then_inc(cl_sum, 1)
            pe.wait_ge(cl_mu, 1)
            column_block(B_V, 0, False)
            pe.wait_ge(qk_ok, 16 + 8)
            for ct in range(CT):
                pe.wait_ge(cl_sq, ct + 1)
                last = nc.tensor.matmul(psum[:, 4, :], ones[:, :], conv_sq[:, ct, :], start=ct == 0, stop=ct == CT - 1)
            last.then_inc(cl_var, 1)
            pe.wait_ge(cl_std, 1)

            def logits(h, s, t):
                if t == 0:
                    pe.wait_ge(qz_ok, h * 2 + 2)
                if not (isinstance(s, int) and s == 0):
                    pe.wait_ge(at_add, s)
                for m in range(2):
                    last = nc.tensor.matmul(psum[:, m, 0:(t + 1) * P], qz[:, m, t * P:(t + 1) * P],
                                            qk[:, bass.ds(h + HEADS, 1), 0:(t + 1) * P].rearrange("p a t -> p (a t)"),
                                            start=True, stop=True)
                last.then_inc(at_log, 1)

            def values(h, s, t):
                pe.wait_ge(at_pt, s + 1)
                if t == 0:
                    pe.wait_ge(at_o, h + 1)
                for j in range(t + 1):
                    last = nc.tensor.matmul(psum[:, 3, t * P:(t + 1) * P], pT[:, t % 2, j * P:(j + 1) * P],
                                            vN[:, j, bass.ds(h * P, P)], start=j == 0, stop=j == t)
                last.then_inc(at_pv, 1)

            def attention_heads(i, last):
                piece = 0
                for k in range(2 * TT):
                    s, t = i * (2 * TT) + k, k % TT
                    for _ in range(FILL[k]):
                        if piece == 0:
                            pe.wait_ge(out_ok, i * 4 + 4)
                        pe.wait_ge(cl_lo, piece + 1)
                        out_piece(i, piece, CT + piece, 4)
                        piece += 1
                    if k > 0:
                        values(i * 2 + (k - 1) // TT, s - 1, (t - 1) % TT)
                    if not (last and k >= 2 * TT - 2):
                        logits(i * 2 + (k + 2) // TT, s + 2, (t + 2) % TT)
                    pe.wait_ge(at_p, s + 1)
                    for j in range(t + 1):
                        end = nc.tensor.transpose(psum[:, 2, j * P:(j + 1) * P],
                                                  ex[:, t % 2, 0, j * P:(j + 1) * P], ident[:, :])
                    end.then_inc(at_tr, 1)
                out_piece(i, HK - 1, CT + HK - 1, 4)
                values(i * 2 + 1, i * (2 * TT) + (2 * TT - 1), TT - 1)

            pe.wait_ge(v_ok, 4)
            logits(0, 0, 0)
            column_block(B_V + 1, 4, False)
            logits(0, 1, 1)
            pe.wait_ge(v_ok, 8)
            with pe.Fori(0, HEADS // 2 - 1) as i:
                attention_heads(i, False)
            attention_heads(HEADS // 2 - 1, True)

            def head_transposes(h):
                pe.wait_ge(fin_n, h + 1)
                if h >= 4:
                    pe.wait_ge(fin_lo, h - 3)
                for t in range(TT):
                    last = nc.tensor.transpose(psum[:, h % 4, t * P:(t + 1) * P], qk[:, h, t * P:(t + 1) * P], ident[:, :])
                last.then_inc(fin_t, 1)

            for h in range(3):
                head_transposes(h)
            pe.wait_ge(out_ok, 4 * 4 + 4)
            for h in range(HEADS):
                if h + 3 < HEADS:
                    head_transposes(h + 3)
                pe.wait_ge(fin_lo, h + 1)
                out_piece(4, h, h, 4)
            for hb in range(5, 8):
                if hb > 5:
                    pe.wait_ge(out_ok, 4 * (hb - 1) + 4)
                for h in range(HEADS):
                    out_piece(hb, h, h, 4 if hb % 2 == 0 else 0)
            def normed(tt):
                pe.wait_ge(ln_y, tt + 1)
                pe.wait_ge(ln_yp, tt + 1)

            transposes(16, acc, normed)
            pe.wait_ge(keys_ld, 16)
            for r in range(4):
                for k in range(4):
                    last = nc.tensor.transpose(psum[:, 4 + r, k * P:(k + 1) * P], keys_in[:, 4 * r + k, :], ident[:, :])
                last.then_inc(keys_t, 1)
            with pe.Fori(0, 2) as i:
                pe.wait_ge(qp_ok, i * 8 + 4)
                column_block(i * 2 + B_WQ, 0, True, 16)
                pe.wait_ge(keys_ok, 4)
                pe.wait_ge(qp_ok, i * 8 + 8)
                column_block(i * 2 + (B_WQ + 1), 4, True, 16)
            pe.wait_ge(qp_ok, 16 + 8)

            for tt in range(TT):
                if tt >= 2:
                    pe.wait_ge(sc_ok, 4 * (tt - 1))
                for hc in range(HC):
                    last = nc.tensor.matmul(psum[:, 4 * (tt % 2) + hc // 4, hc % 4 * P:(hc % 4 + 1) * P],
                                            qp[:, hc, tt * P:(tt + 1) * P], keysT[:, hc, :], start=True, stop=True)
                    if hc % 4 == 3:
                        last.then_inc(sc_ps, 1)
            pe.wait_ge(sc_ok, 4 * TT)

            def pick_transposes(tt):
                pe.wait_ge(rt, RT_STEPS * tt + 135)
                for n in range(3):
                    last = nc.tensor.transpose(psum[:, 2, n * P:(n + 1) * P], ij[:, n, :], ident[:, :])
                last.then_inc(pick_t, 1)

            def gate_tables(quad, tt, b):
                pe.wait_ge(hot_ok, quad + (tt * 32 + 1))
                pe.wait_ge(g_ev, quad + (tt * 32 + 1))
                for t in range(4):
                    nc.tensor.matmul(psum[:, 2 * b + t // 2, t % 2 * 2 * NK:(t % 2 + 1) * 2 * NK], hot_j[:, b, t, :],
                                     hot_i[:, b, t, :, :], start=True, stop=True).then_inc(g_mm, 1)

            def u_transposes(n, c, kq, freed=ut_raw):
                if kq == 0:
                    pe.wait_ge(u_ld[c % 2], n_loads(n, c))
                pe.wait_ge(freed, n * 4 + (kq + 1))
                for kk in range(4):
                    last = nc.tensor.transpose(psum[:, 4 + kq % 2, kk * P:(kk + 1) * P],
                                               u_in[:, c % 2, (4 * kq + kk) * P:(4 * kq + kk + 1) * P], ident[:, :])
                last.then_inc(ut_ps, 1)

            def n_loads(n, c):
                return (n - (c % 2)) * 8 + 16

            def u_products(n, c, kq):
                pe.wait_ge(ut_lo, n * 4 + (kq + 3))
                if kq == 0:
                    pe.wait_ge(gelu_ok, n + 1)
                for kk in range(4):
                    for m, (ui, ai) in enumerate(PRODUCTS):
                        last = nc.tensor.matmul(psum[:, 6 + c % 2, :], utT[:, kq, ui, kk, :], actT[:, ai, 4 * kq + kk, :],
                                                start=(kq == 0 and kk == 0 and m == 0),
                                                stop=(kq == 3 and kk == 3 and m == 2))
                last.then_inc(ut_used, 1)

            def u_chunk(n, c, last=False, tables=None, freed=ut_raw, freed_next=ut_raw):
                u_products(n, c, 0)
                if tables:
                    tables(0)
                u_transposes(n, c, 2, freed)
                u_products(n, c, 1)
                if tables:
                    tables(1)
                u_transposes(n, c, 3, freed)
                u_products(n, c, 2)
                if tables:
                    tables(2)
                if not last:
                    u_transposes(n + 1, (c + 1) % 4, 0, freed_next)
                u_products(n, c, 3)
                if tables:
                    tables(3)
                if not last:
                    u_transposes(n + 1, (c + 1) % 4, 1, freed_next)

            def v_stage(g, c):
                for j in range(PIECES):
                    pe.wait_ge(piece_lo, (g + BLOCKS) * KT + (c * PIECES + j + 1))
                    if c == 0:
                        pe.wait_ge(w_lo, g * 4 + (j + 5))
                    for tt in range(TT):
                        if j == 0:
                            pe.wait_ge(v_added, (g * 4 + c) * 4 + (tt + 1))
                        for m, (wi, vi) in enumerate(PRODUCTS):
                            last = nc.tensor.matmul(psum[:, tt, :], w_hl[:, j, wi, tt * P:(tt + 1) * P], hl_v[:, j, vi, :],
                                                    start=(j == 0 and m == 0), stop=(j == PIECES - 1 and m == 2))
                        if j == PIECES - 1 and tt < TT - 1:
                            last.then_inc(v_ready, 1)
                    last.then_inc(piece_used, 1)

            u_transposes(0, 0, 0)
            u_transposes(0, 0, 1)
            n0 = 0
            for tt in range(TT):
                with pe.Fori(0, ROUTE_CHUNKS // 2) as i:
                    for c in range(2):
                        u_chunk(i * 2 + (n0 + c), c)
                n0 += ROUTE_CHUNKS
                pick_transposes(tt)
                with pe.Fori(0, GATE_CHUNKS // 2) as i:
                    for c in range(2):
                        def tables(part):
                            gate_tables(i * (2 * QUADS) + (c * QUADS + part), tt, part % 2)
                        u_chunk(i * 2 + (n0 + c), c, tables=tables)
                n0 += GATE_CHUNKS
            with pe.Fori(0, STORE_CHUNKS // 2) as i:
                for c in range(2):
                    u_chunk(i * 2 + (n0 + c), c)
            with pe.Fori(0, GROUPS - AHEAD_GROUPS - 1) as g:
                for c in range(4):
                    u_chunk(g * 4 + (AHEAD + c), c, freed=ut_lo, freed_next=ut_lo)
                    v_stage(g, c)
            g = GROUPS - AHEAD_GROUPS - 1
            for c in range(4):
                u_chunk(g * 4 + AHEAD + c, c, last=c == 3, freed=ut_lo, freed_next=ut_lo)
                v_stage(g, c)
            with pe.Fori(GROUPS - AHEAD_GROUPS, GROUPS) as g:
                for c in range(4):
                    v_stage(g, c)

        @block.vector
        def _(dve):
            dve.sem_inc(glu_ok, 4)
            dve.sem_inc(conv_step, 1)
            dve.sem_inc(out_ok, 4)
            dve.sem_inc(ut_lo, 2)
            dve.sem_inc(ut_raw, 2)
            dve.sem_inc(g_ev, 2)
            dve.sem_inc(w_made, 4)
            dve.sem_inc(v_added, 4)
            def transposed_lows(base):
                for u in range(TT * 4):
                    tt, kq = u // 4, u % 4
                    at = (slice(None), slice(4 * kq, 4 * kq + 4), slice(tt * P, (tt + 1) * P))
                    dve.wait_ge(tr_hi, base + u + 1)
                    nc.vector.tensor_tensor(actT[:, 1, at[1], at[2]], psum[:, u % 4, :].rearrange("p (k t) -> p k t", k=4),
                                            actT[:, 0, at[1], at[2]].bitcast(F32), ALU.subtract).then_inc(tr_lo, 1)

            transposed_lows(0)
            dve.wait_ge(par_in, PARAMS)
            nc.vector.memset(bv[:, 0:P - 1], MASKED)
            nc.vector.tensor_copy(bv[:, P - 1:P - 1 + MAX_EXACT], rel_t[:, 0:MAX_EXACT])
            for b, span in enumerate(bucket_ranges()):
                if b >= MAX_EXACT and span:
                    n = span[1] - span[0] + 1
                    nc.vector.tensor_copy(bv[:, P - 1 + span[0]:P - 1 + span[0] + n],
                                          bass.AP(rel_t, b, [[BUCKETS, HEADS], [0, n]]))
            nc.vector.memset(bv[:, SPAN:BV], 0.0).then_inc(bv_built, 1)
            nc.vector.tensor_tensor(lam_pr[:, :, :], lam_in[:, 0:4:2, :], lam_in[:, 1:4:2, :], ALU.mult).then_inc(lam_step, 1)
            dve.wait_ge(lam_step, 1)
            nc.vector.reduce_sum(lam_s[:, :], lam_pr[:, :, :], AX_X).then_inc(lam_step, 1)
            nc.vector.tensor_scalar(sub_g[:, :], sub_g[:, :], 1.0 - LAMBDA_INIT, None, ALU.mult)
            nc.vector.memset(conv_in[:, :, 0:TAPS - 1], 0.0).then_inc(conv_pad, 1)
            dve.wait_ge(lam_exp, 1)
            nc.vector.tensor_tensor(neg_lam[:, :], lam_s[:, 1:2], lam_s[:, 0:1], ALU.subtract).then_inc(lam_step, 1)
            dve.wait_ge(lam_step, 3)
            nc.vector.tensor_scalar(neg_lam[:, :], neg_lam[:, :], -LAMBDA_INIT, None, ALU.add).then_inc(lam_step, 1)
            dve.wait_ge(lam_step, 4)
            dve.wait_ge(chan_ok, 1)
            dve.wait_ge(conv_pad, 1)
            conv = Steps(dve, conv_step, 1)
            with conv.loop(0, 2, 4 * TAPS) as j:
                conv.wait()
                for c in range(4):
                    dve.wait_ge(sig_ok, j * 4 + (c + 5))
                    wait_bank(dve, j * 2 + 1, c)
                    nc.vector.scalar_tensor_tensor(conv_in[:, c, TAPS - 1:], psum[:, 4 + c, :],
                                                   chan[:, bass.ds(j * 4 + c, 1), TAPS + 3:TAPS + 4].rearrange("p a b -> p (a b)"),
                                                   sig[:, c, :], ALU.add, ALU.mult).then_inc(glu_ok, 1)
                for c in range(4):
                    dve.wait_ge(glu_ok, j * 4 + (c + 5))
                    ch = chan[:, bass.ds(j * 4 + c, 1), :].rearrange("p a b -> p (a b)")
                    conv(nc.vector.tensor_scalar(conv_y[:, bass.ds(j * 4 + c, 1), :].rearrange("p a t -> p (a t)"),
                                                 conv_in[:, c, 0:T], ch[:, 0:1], ch[:, TAPS:TAPS + 1], ALU.mult, ALU.add))
                with conv.loop(1, TAPS, 4) as tap:
                    for c in range(4):
                        y = conv_y[:, bass.ds(j * 4 + c, 1), :].rearrange("p a t -> p (a t)")
                        conv.wait(3)
                        conv(nc.vector.scalar_tensor_tensor(
                            y, conv_in[:, c, bass.ds(tap, T)],
                            chan[:, bass.ds(j * 4 + c, 1), bass.ds(tap, 1)].rearrange("p a b -> p (a b)"),
                            y, ALU.mult, ALU.add))
            dve.wait_ge(cl_mu, 1)
            for ct in range(CT):
                nc.vector.tensor_tensor(conv_y[:, ct, :], conv_y[:, ct, :], conv_mu[:, :], ALU.subtract).then_inc(cl_sub, 1)
            dve.wait_ge(cl_std, 1)
            nc.vector.reciprocal(conv_std[:, :], conv_std[:, :]).then_inc(cl_rstd, 1)
            dve.wait_ge(cl_rstd, 1)
            for ct in range(CT):
                dve.wait_ge(cl_sq, ct + 1)
                nc.vector.tensor_tensor(conv_y[:, ct, :], conv_y[:, ct, :], conv_std[:, :], ALU.mult).then_inc(cl_mul, 1)

            def add_bias(i, s, t, slot):
                n = (t + 1) * P
                if t == 0:
                    dve.wait_ge(bias_in[slot], i * 16 + 16)
                dve.wait_ge(at_log, s + 5)
                if not (isinstance(s, int) and s == 0):
                    dve.wait_ge(at_tr, s)
                row = bass.AP(bias_t, slot * T + n - 1, [[2 * T, P], [0, 2], [-1, n]])
                nc.vector.tensor_tensor(ex[:, t % 2, :, 0:n], psum[:, 0:2, 0:n], row,
                                        ALU.add).then_inc(at_add, 1)

            def maxima(s, t):
                dve.wait_ge(at_add, s + 1)
                nc.vector.tensor_reduce(neg_max[:, t % 2, :], ex[:, t % 2, :, 0:(t + 1) * P], AX_X, ALU.max,
                                        negate=True).then_inc(at_max, 1)

            def start_residual(hb):
                for tt in range(TT):
                    wait_half(dve, hb, tt)
                    cols = acc[:, tt, bass.ds(hb * CB, CB)]
                    nc.vector.scalar_tensor_tensor(cols, cols, ALPHA, psum[:, 4 + tt, :], ALU.mult, ALU.add).then_inc(out_ok, 1)

            def attention_heads(i, last):
                for k in range(2 * TT):
                    s, t, b = i * (2 * TT) + k, k % TT, k % 2
                    n = (t + 1) * P
                    more = not (last and k == 2 * TT - 1)
                    dve.wait_ge(at_exp, s * 2 + 2)
                    nc.vector.reciprocal(rsum[:, b, :], esum[:, b, :]).then_inc(at_rz, 1)
                    if more:
                        k1 = k + 1
                        add_bias(i + k1 // (2 * TT), s + 1, k1 % TT, k1 // TT % 2)
                    dve.wait_ge(at_rz, s + 1)
                    nc.vector.tensor_tensor(rsum[:, b, 1:2], rsum[:, b, 1:2], neg_lam[:, :], ALU.mult).then_inc(at_rl, 1)
                    if more:
                        maxima(s + 1, (k + 1) % TT)
                    dve.wait_ge(at_rl, s + 1)
                    nc.vector.tensor_scalar(ex[:, b, 1, 0:n], ex[:, b, 1, 0:n], rsum[:, b, 1:2], None,
                                            ALU.mult).then_inc(at_e1, 1)
                    dve.wait_ge(at_e1, s + 1)
                    nc.vector.scalar_tensor_tensor(ex[:, b, 0, 0:n], ex[:, b, 0, 0:n], rsum[:, b, 0:1], ex[:, b, 1, 0:n],
                                                   ALU.mult, ALU.add).then_inc(at_p, 1)
                dve.wait_ge(x_again, TT * 16)
                start_residual(i)

            add_bias(0, 0, 0, 0)
            maxima(0, 0)
            with dve.Fori(0, HEADS // 2 - 1) as i:
                attention_heads(i, False)
            attention_heads(HEADS // 2 - 1, True)
            dve.wait_ge(fin_std, 1)
            nc.vector.reciprocal(ms[:, :], ms[:, :]).then_inc(fin_r, 1)
            dve.wait_ge(fin_r, 1)

            def head_scale(h):
                o = qk[:, h, :].rearrange("p (t d) -> p t d", t=TT)
                r = bass.AP(ms, h * TT, [[HEADS * TT, P], [1, TT], [0, P]])
                nc.vector.tensor_tensor(o, o, r, ALU.mult).then_inc(fin_n, 1)

            head_scale(0)
            for h in range(HEADS):
                if h + 1 < HEADS:
                    head_scale(h + 1)
                dve.wait_ge(fin_hi, h + 1)
                nc.vector.scalar_tensor_tensor(actT[:, 1, h, :], psum[:, h % 4, :], sub_g[:, 0:1],
                                               actT[:, 0, h, :].bitcast(F32), ALU.mult, ALU.subtract).then_inc(fin_lo, 1)

            for hb in range(4, 8):
                cols = slice((hb - 4) * CB, (hb - 3) * CB)
                bank = 4 if hb % 2 == 0 else 0
                for tt in range(TT):
                    wait_half(dve, hb, tt)
                    dve.wait_ge(out_ok, 4 * (hb - 4) + tt + 1 + 4)
                    nc.vector.tensor_tensor(acc[:, tt, cols], acc[:, tt, cols], psum[:, bank + tt, :], ALU.add).then_inc(out_ok, 1)
                for tt in range(TT):
                    dve.wait_ge(out_ok, 4 * hb + tt + 1 + 4)
                    nc.vector.bn_stats(ln_stats[:, tt, hb - 4, :], acc[:, tt, cols]).then_inc(ln_stat, 1)

            def layer_norm(which, gb, gb_sem):
                dve.wait_ge(ln_stat, 20 * which + 16)
                for tt in range(TT):
                    nc.vector.bn_aggr(ln_mv[:, tt, :], ln_stats[:, tt, :, :].rearrange("p a s -> p (a s)")).then_inc(ln_stat, 1)
                dve.wait_ge(ln_std, which + 1)
                nc.vector.reciprocal(ln_rstd[:, :, :], ln_rstd[:, :, :]).then_inc(ln_r, 1)
                dve.wait_ge(ln_r, 2 * which + 1)
                nc.vector.scalar_tensor_tensor(ln_shift[:, :, :], ln_mv[:, :, 0:1], -1.0, ln_rstd[:, :, :],
                                               ALU.mult, ALU.mult).then_inc(ln_r, 1)
                dve.wait_ge(gb_sem, 32)
                for tt in range(TT):
                    a = acc[:, tt, 0:LN_DVE]
                    nc.vector.scalar_tensor_tensor(a, a, ln_mv[:, tt, 0:1], gb[:, 0, 0:LN_DVE],
                                                   ALU.subtract, ALU.mult).then_inc(ln_c, 1)
                    dve.wait_ge(ln_c, TT * which + tt + 1)
                    nc.vector.scalar_tensor_tensor(a, a, ln_rstd[:, tt, :], gb[:, 1, 0:LN_DVE],
                                                   ALU.mult, ALU.add).then_inc(ln_y, 1)

            layer_norm(0, gb1, gb_in)
            transposed_lows(16)

            route = Steps(dve, rt)

            def top16(values, spare, best, where, n):
                for r in range(n):
                    route(nc.vector.max(best[:, r, 0:8], values[:, r, :]))
                route.wait()
                for r in range(n):
                    route(nc.vector.match_replace(spare[:, r, :], best[:, r, 0:8], values[:, r, :], TAKEN))
                route.wait()
                for r in range(n):
                    route(nc.vector.max(best[:, r, 8:16], spare[:, r, :]))
                for r in range(n):
                    route(nc.vector.max_index(where[:, r, 0:8], best[:, r, 0:8], values[:, r, :]))
                route.wait()
                for r in range(n):
                    route(nc.vector.max_index(where[:, r, 8:16], best[:, r, 8:16], spare[:, r, :]))

            flat = PH * TOPK * TOPK
            spare3 = sc2[:, :, :].rearrange("p h n -> p (h n)").rearrange("p (h n) -> p h n", h=PH)
            pairs4 = sc2[:, :, :].rearrange("p h n -> p (h n)").rearrange("p (h k a) -> p h k a", h=PH, k=TOPK)
            def route_tile(tt):
                dve.wait_ge(sc_in, tt * 16 + 16)
                top16(sc, sc2, top_v, top_i, HC)
                route.wait()
                first = bass.AP(top_v, 0, [[HC * TOPK, P], [2 * TOPK, PH], [1, TOPK], [0, TOPK]])
                second = bass.AP(top_v, TOPK, [[HC * TOPK, P], [2 * TOPK, PH], [0, TOPK], [1, TOPK]])
                route(nc.vector.tensor_tensor(cand[:, :, :].rearrange("p h (a b) -> p h a b", a=TOPK), first, second, ALU.add))
                route.wait()
                top16(cand, spare3, best_v, best_c, PH)
                route.wait()
                route(nc.vector.tensor_copy(top_f[:, :, :], top_i[:, :, :]))
                head_max = bass.AP(best_v, 0, [[PH * TOPK, P], [TOPK, PH], [0, TOPK]])
                route(nc.vector.tensor_tensor(ij[:, 2, :].rearrange("p (h k) -> p h k", h=PH), best_v[:, :, :], head_max,
                                              ALU.subtract))
                route(nc.vector.tensor_scalar(pick_u[:, 0, :, :], best_c[:, :, :], 4, None, ALU.logical_shift_right))
                route(nc.vector.tensor_scalar(pick_u[:, 1, :, :], best_c[:, :, :], 15, None, ALU.bitwise_and))
                route.wait()
                route(nc.vector.tensor_copy(pick_f[:, :, :, :], pick_u[:, :, :, :]))
                for half in range(2):
                    route.wait()
                    place_ = bass.AP(pick_f, half * PH * TOPK, [[2 * PH * TOPK, P], [1, PH * TOPK], [0, TOPK]])
                    slots = bass.AP(iota_top, 0, [[TOPK, P], [0, PH * TOPK], [1, TOPK]])
                    names = bass.AP(top_f, half * TOPK, [[HC * TOPK, P], [2 * TOPK, PH], [0, TOPK], [1, TOPK]])
                    route(nc.vector.tensor_tensor(pairs4.rearrange("p h k a -> p (h k) a"), place_, slots, ALU.is_equal))
                    route.wait()
                    route(nc.vector.tensor_tensor(pairs4, pairs4, names, ALU.mult))
                    route.wait()
                    route(nc.vector.reduce_sum(ij[:, half, :], pairs4.rearrange("p h k a -> p (h k) a"), AX_X))
                dve.wait_ge(g_exp, tt + 1)
                e3 = ij[:, 2, :].rearrange("p (h k) -> p h k", h=PH)
                route(nc.vector.reduce_sum(gsum[:, 0, :], e3, AX_X))
                route.wait()
                route(nc.vector.reciprocal(gsum[:, 1, :], gsum[:, 0, :]))
                route.wait()
                route(nc.vector.tensor_tensor(e3, e3, bass.AP(gsum, PH, [[2 * PH, P], [1, PH], [0, TOPK]]), ALU.mult))
                dve.wait_ge(pick_t, tt + 1)
                route(nc.vector.tensor_copy(picks[:, :, :], psum[:, 2, 0:3 * P].rearrange("p (n t) -> p n t", n=3)))
                route.wait()
                route(nc.vector.tensor_copy(gate_hl[:, 0, :], picks[:, 2, :]))
                route.wait()
                route(nc.vector.tensor_tensor(gate_hl[:, 1, :], picks[:, 2, :], gate_hl[:, 0, :].bitcast(F32), ALU.subtract))

            def hot_rows(quad, tt, b):
                dve.wait_ge(g_mm, quad * 4 + (tt * P + 4))
                i_row = bass.AP(iota_row, 0, [[P, P], [0, 4], [1, P]])
                j_of = bass.AP(picks, quad * 4 + P, [[3 * P, P], [1, 4], [0, P]])
                nc.vector.tensor_tensor(hot_j[:, b, :, :], i_row, j_of, ALU.is_equal)
                for t in range(4):
                    at = bass.ds(quad * 4 + t, 1)
                    for part in range(2):
                        last = nc.vector.tensor_scalar(hot_i[:, b, t, part, :], iota_row[:, :], picks[:, 0, at],
                                                       gate_hl[:, part, at].bitcast(F32), ALU.is_equal, ALU.mult)
                last.then_inc(hot_ok, 1)

            def keep_gates(quad, tt, b):
                dve.wait_ge(table_lo_ok, quad + (tt * 32 + 1))
                hi = psum[:, 2 * b:2 * b + 2, :].rearrange("p b (t h i) -> p (b t) h i", t=2, h=2)[:, :, 0, :]
                nc.vector.tensor_tensor(gbuf[:, :, bass.ds(quad * 4, 4)].rearrange("p i t -> p t i"), hi,
                                        table_lo[:, b, :, :], ALU.add).then_inc(g_ev, 1)

            for tt in range(TT):
                route_tile(tt)
                assert route.total == RT_STEPS * (tt + 1)
                route.wait()
                for b in range(2):
                    hot_rows(b, tt, b)
                if tt:
                    for r in range(4):
                        dve.wait_ge(g_out[r], 16 * tt)
                with dve.Fori(0, P // 8 - 1) as i:
                    for b in range(2):
                        keep_gates(i * 2 + b, tt, b)
                        hot_rows(i * 2 + (b + 2), tt, b)
                for b in range(2):
                    keep_gates(P // 4 - 2 + b, tt, b)

            def u_low(n, kq):
                dve.wait_ge(ut_hi, n * 4 + (kq + 1))
                nc.vector.tensor_tensor(utT[:, kq, 1, :, :], psum[:, 4 + kq % 2, :].rearrange("p (k e) -> p k e", k=4),
                                        utT[:, kq, 0, :, :].bitcast(F32), ALU.subtract).then_inc(ut_lo, 1)

            def gate(m, c):
                dve.wait_ge(act_ld[c], m * 4 + (16 - 4 * c))
                dve.wait_ge(g_ld[c], m * 4 + (16 - 4 * c))
                nc.vector.tensor_tensor(act_in[:, c, :], act_in[:, c, :], gate_in[:, c, :], ALU.mult).then_inc(w_made, 1)

            def accumulate(g, c):
                for tt in range(TT):
                    dve.wait_ge(res_in, TT * 16)
                    v = g * 4 + c
                    if tt < TT - 1:
                        dve.wait_ge(v_ready, v * 3 + (tt + 1))
                    else:
                        dve.wait_ge(piece_used, v * PIECES + (BLOCKS * KT + 2 * PIECES))
                    a = acc[:, tt, c * CB:(c + 1) * CB]
                    nc.vector.tensor_tensor(a, a, psum[:, tt, :], ALU.add).then_inc(v_added, 1)

            dve.wait_ge(ut_lo, AHEAD * 4 + 2)
            u_low(AHEAD, 0)
            u_low(AHEAD, 1)
            for c in range(4):
                gate(c, c)
            def expert_group(g, with_u, last_u):
                for c in range(4):
                    n = g * 4 + (AHEAD + c)
                    if with_u:
                        u_low(n, 2)
                        u_low(n, 3)
                        if not (last_u and c == 3):
                            u_low(n + 1, 0)
                            u_low(n + 1, 1)
                    gate(g * 4 + (4 + c), c)
                    accumulate(g, c)

            with dve.Fori(0, GROUPS - AHEAD_GROUPS - 1) as g:
                expert_group(g, True, False)
            expert_group(GROUPS - AHEAD_GROUPS - 1, True, True)
            with dve.Fori(GROUPS - AHEAD_GROUPS, GROUPS - 1) as g:
                expert_group(g, False, False)
            for c in range(4):
                accumulate(GROUPS - 1, c)
                for tt in range(TT):
                    dve.wait_ge(v_added, (GROUPS * 4 - 4 + c) * 4 + tt + 1 + 4)
                    nc.vector.bn_stats(ln_stats[:, tt, c, :], acc[:, tt, c * CB:(c + 1) * CB]).then_inc(ln_stat, 1)
            layer_norm(1, gb2, ln2_in)


_INS = ["x", "w_in", "b_glu", "conv_w", "conv_b", "conv_ln_g", "conv_ln_b", "lambda_q1", "lambda_k1", "lambda_q2",
        "lambda_k2", "subln_g", "rel_bias", "w_out", "ln1_g", "ln1_b", "peer_wq", "peer_keys", "peer_u", "peer_v",
        "ln2_g", "ln2_b"]


def kernel(**inputs):
    import concourse.bacc as bacc
    from concourse.bass_utils import run_bass_kernel_spmd

    nc = bacc.Bacc("TRN2", target_bir_lowering=False, num_devices=1)
    arrays, args = {}, []
    for name in _INS:
        a = np.ascontiguousarray(inputs[name])
        arrays[f"in_{name}"] = a
        args.append(nc.dram_tensor(f"in_{name}", a.shape, mybir.dt.from_np(a.dtype), kind="ExternalInput").ap())
    out = nc.dram_tensor("out", (1, T, D), F32, kind="ExternalOutput").ap()
    layer(nc, *args, out)
    result = run_bass_kernel_spmd(nc, [arrays], core_ids=[0])
    return result.results[0]["out"]
```
